# Optimizing a Trainium2 kernel written in Bass

```python
import math
import jax, jax.numpy as jnp
from jax import lax
import numpy as np

D_MODEL = 1024
BATCH = 1
SEQ = 1024
DEPTH = 2
DEC_BATCH = 8
DEC_SEQ = 4
PAST_LEN = 256
PAGE_SIZE = 128

N_A_LAYERS = DEPTH // 2
N_B_LAYERS = DEPTH - N_A_LAYERS
N_HEADS = 16
HEAD_DIM = D_MODEL // N_HEADS
CONV_WIDTH = 31
D_FF = 256 * math.ceil(8 * D_MODEL / (3 * 256))
Q_BLOCK = 128
LOGIT_BIAS_INIT = -6.0
RMS_EPS = 1e-6
LN_EPS = 1e-5

kernel_name = 'yoco_conformer_conv_stick_breaking_step'

def rms_norm(x, g):
    xf = x.astype(jnp.float32)
    y = xf * lax.rsqrt(jnp.mean(xf * xf, axis=-1, keepdims=True) + RMS_EPS)
    return (y * g.astype(jnp.float32)).astype(x.dtype)

def layer_norm(x, g, b):
    xf = x.astype(jnp.float32)
    mu = jnp.mean(xf, axis=-1, keepdims=True)
    xc = xf - mu
    y = xc * lax.rsqrt(jnp.mean(xc * xc, axis=-1, keepdims=True) + LN_EPS)
    return (y * g.astype(jnp.float32) + b.astype(jnp.float32)).astype(x.dtype)

def swiglu(h, w_gate, w_up, w_down):
    return (jax.nn.silu(h @ w_gate) * (h @ w_up)) @ w_down

def conformer_conv(h, buf, w_pw1, b_pw1, w_dw, b_dw, ln_g, ln_b, w_pw2, b_pw2):
    a = h @ w_pw1 + b_pw1
    d = a.shape[-1] // 2
    u = a[..., :d] * jax.nn.sigmoid(a[..., d:])
    full = jnp.concatenate([buf.astype(u.dtype), u], axis=1)
    new_buf = full[:, full.shape[1] - (CONV_WIDTH - 1):]
    c = lax.conv_general_dilated(
        full, w_dw[:, None, :].astype(u.dtype), window_strides=(1,), padding='VALID',
        dimension_numbers=('NWC', 'WIO', 'NWC'), feature_group_count=d) + b_dw
    c = jax.nn.silu(layer_norm(c, ln_g, ln_b))
    return c @ w_pw2 + b_pw2, new_buf

def stick_breaking_weights(z, mask):
    log_beta = jax.nn.log_sigmoid(z)
    log_1m = jnp.where(mask, jax.nn.log_sigmoid(-z), 0.0)
    ax = z.ndim - 1
    tail = lax.cumsum(log_1m, axis=ax, reverse=True) - log_1m
    return jnp.where(mask, jnp.exp(log_beta + tail), 0.0)

def stick_breaking_prompt(q, k, v, bias):
    b, t, h, dh = q.shape
    nb = t // Q_BLOCK
    scale = 1.0 / math.sqrt(dh)
    q_blocks = q.reshape(b, nb, Q_BLOCK, h, dh).transpose(1, 0, 2, 3, 4)
    kpos = jnp.arange(t)
    bias_f = bias.astype(jnp.float32)[None, :, None, None]

    def block(args):
        q_blk, start = args
        z = jnp.einsum('bqhd,bkhd->bhqk', q_blk, k,
                       preferred_element_type=jnp.float32) * scale + bias_f
        qpos = start + jnp.arange(Q_BLOCK)
        mask = kpos[None, :] < qpos[:, None]
        a = stick_breaking_weights(z, mask)
        return jnp.einsum('bhqk,bkhd->bqhd', a, v.astype(jnp.float32)).astype(q.dtype)

    out = lax.map(block, (q_blocks, jnp.arange(nb) * Q_BLOCK))
    return out.transpose(1, 0, 2, 3, 4).reshape(b, t, h, dh)

def stick_breaking_sample(q, k_new, v_new, k_past, v_past, bias):
    p = k_past.shape[1]
    tn = q.shape[1]
    scale = 1.0 / math.sqrt(q.shape[-1])
    z = jnp.concatenate([
        jnp.einsum('bqhd,bkhd->bhqk', q, k_past, preferred_element_type=jnp.float32),
        jnp.einsum('bqhd,bkhd->bhqk', q, k_new, preferred_element_type=jnp.float32)],
        axis=-1) * scale + bias.astype(jnp.float32)[None, :, None, None]
    kpos = jnp.arange(p + tn)
    qpos = p + jnp.arange(tn)
    mask = kpos[None, :] < qpos[:, None]
    a = stick_breaking_weights(z, mask)
    out = (jnp.einsum('bhqk,bkhd->bqhd', a[..., :p], v_past.astype(jnp.float32))
           + jnp.einsum('bhqk,bkhd->bqhd', a[..., p:], v_new.astype(jnp.float32)))
    return out.astype(q.dtype)

def setup_inputs(seed: int = 0) -> dict:
    key = jax.random.key(seed)
    ks = jax.random.split(key, 32)
    f32 = jnp.float32
    n_pages = PAST_LEN // PAGE_SIZE
    n_used = DEC_BATCH * n_pages
    n_phys = n_used + max(1, n_used // 4)
    hd = N_HEADS * HEAD_DIM

    def nrm(k, shape, scale=1.0):
        return jax.random.normal(k, shape, f32) * scale

    page_table = jax.random.permutation(ks[5], n_phys)[:n_used].reshape(DEC_BATCH, n_pages).astype(jnp.int32)
    return {
        'x_prompt': nrm(ks[0], (BATCH, SEQ, D_MODEL)),
        'x_sample': nrm(ks[1], (DEC_BATCH, DEC_SEQ, D_MODEL)),
        'state_conv': nrm(ks[2], (N_A_LAYERS, DEC_BATCH, CONV_WIDTH - 1, D_MODEL), 0.5),
        'cache_k': nrm(ks[3], (n_phys, PAGE_SIZE, N_HEADS, HEAD_DIM)),
        'cache_v': nrm(ks[4], (n_phys, PAGE_SIZE, N_HEADS, HEAD_DIM)),
        'page_table': page_table,
        'norm_mix': 1.0 + nrm(ks[6], (DEPTH, D_MODEL), 0.02),
        'norm_ffn': 1.0 + nrm(ks[7], (DEPTH, D_MODEL), 0.02),
        'conv_w_pw1': nrm(ks[8], (N_A_LAYERS, D_MODEL, 2 * D_MODEL), D_MODEL ** -0.5),
        'conv_b_pw1': nrm(ks[9], (N_A_LAYERS, 2 * D_MODEL), 0.02),
        'conv_w_dw': nrm(ks[10], (N_A_LAYERS, CONV_WIDTH, D_MODEL), CONV_WIDTH ** -0.5),
        'conv_b_dw': nrm(ks[11], (N_A_LAYERS, D_MODEL), 0.02),
        'conv_ln_g': 1.0 + nrm(ks[12], (N_A_LAYERS, D_MODEL), 0.02),
        'conv_ln_b': nrm(ks[13], (N_A_LAYERS, D_MODEL), 0.02),
        'conv_w_pw2': nrm(ks[14], (N_A_LAYERS, D_MODEL, D_MODEL), D_MODEL ** -0.5),
        'conv_b_pw2': nrm(ks[15], (N_A_LAYERS, D_MODEL), 0.02),
        'kv_norm': 1.0 + nrm(ks[16], (D_MODEL,), 0.02),
        'w_kv': nrm(ks[17], (D_MODEL, 2 * hd), D_MODEL ** -0.5),
        'w_q': nrm(ks[18], (N_B_LAYERS, D_MODEL, hd), 0.5 * D_MODEL ** -0.5),
        'w_o': nrm(ks[19], (N_B_LAYERS, hd, D_MODEL), hd ** -0.5),
        'b_logit': LOGIT_BIAS_INIT + nrm(ks[24], (N_B_LAYERS, N_HEADS), 0.5),
        'ffn_w_gate': nrm(ks[20], (DEPTH, D_MODEL, D_FF), D_MODEL ** -0.5),
        'ffn_w_up': nrm(ks[21], (DEPTH, D_MODEL, D_FF), D_MODEL ** -0.5),
        'ffn_w_down': nrm(ks[22], (DEPTH, D_FF, D_MODEL), D_FF ** -0.5),
        'final_norm': 1.0 + nrm(ks[23], (D_MODEL,), 0.02),
    }

def reference(x_prompt, x_sample, state_conv, cache_k, cache_v, page_table,
              norm_mix, norm_ffn, conv_w_pw1, conv_b_pw1, conv_w_dw, conv_b_dw,
              conv_ln_g, conv_ln_b, conv_w_pw2, conv_b_pw2, kv_norm, w_kv, w_q, w_o,
              b_logit, ffn_w_gate, ffn_w_up, ffn_w_down, final_norm):
    xp, xs = x_prompt, x_sample
    dec_b, n_pages = page_table.shape
    hd = N_HEADS * HEAD_DIM

    k_past = cache_k[page_table].reshape(dec_b, n_pages * PAGE_SIZE, N_HEADS, HEAD_DIM)
    v_past = cache_v[page_table].reshape(dec_b, n_pages * PAGE_SIZE, N_HEADS, HEAD_DIM)

    def shared_kv(x):
        kv = rms_norm(x, kv_norm) @ w_kv
        b, t = x.shape[0], x.shape[1]
        return (kv[..., :hd].reshape(b, t, N_HEADS, HEAD_DIM),
                kv[..., hd:].reshape(b, t, N_HEADS, HEAD_DIM))

    conv_bufs_p, conv_bufs_s = [], []
    k_p = v_p = k_s = v_s = None
    for l in range(DEPTH):
        if l < N_A_LAYERS:
            prm = (conv_w_pw1[l], conv_b_pw1[l], conv_w_dw[l], conv_b_dw[l],
                   conv_ln_g[l], conv_ln_b[l], conv_w_pw2[l], conv_b_pw2[l])
            zero_buf = jnp.zeros((xp.shape[0], CONV_WIDTH - 1, xp.shape[-1]), xp.dtype)
            hp, bp = conformer_conv(rms_norm(xp, norm_mix[l]), zero_buf, *prm)
            hs, bs = conformer_conv(rms_norm(xs, norm_mix[l]), state_conv[l], *prm)
            conv_bufs_p.append(bp)
            conv_bufs_s.append(bs)
        else:
            if l == N_A_LAYERS:
                k_p, v_p = shared_kv(xp)
                k_s, v_s = shared_kv(xs)
            j = l - N_A_LAYERS
            qp = (rms_norm(xp, norm_mix[l]) @ w_q[j]).reshape(xp.shape[0], xp.shape[1], N_HEADS, HEAD_DIM)
            qs = (rms_norm(xs, norm_mix[l]) @ w_q[j]).reshape(xs.shape[0], xs.shape[1], N_HEADS, HEAD_DIM)
            op = stick_breaking_prompt(qp, k_p, v_p, b_logit[j])
            os_ = stick_breaking_sample(qs, k_s, v_s, k_past, v_past, b_logit[j])
            hp = op.reshape(xp.shape[0], xp.shape[1], hd) @ w_o[j]
            hs = os_.reshape(xs.shape[0], xs.shape[1], hd) @ w_o[j]
        xp = xp + hp
        xs = xs + hs
        xp = xp + swiglu(rms_norm(xp, norm_ffn[l]), ffn_w_gate[l], ffn_w_up[l], ffn_w_down[l])
        xs = xs + swiglu(rms_norm(xs, norm_ffn[l]), ffn_w_gate[l], ffn_w_up[l], ffn_w_down[l])

    y_prompt = rms_norm(xp, final_norm)
    y_sample = rms_norm(xs, final_norm)
    state_conv_prompt = jnp.stack(conv_bufs_p, axis=0)
    state_conv_sample = jnp.stack(conv_bufs_s, axis=0)
    return (y_prompt, y_sample, state_conv_prompt, state_conv_sample, k_p, v_p, k_s, v_s)


_drawn_inputs = setup_inputs


def setup_inputs(seed=0):
    import zlib

    import numpy as np

    out = dict(_drawn_inputs(seed))
    spreads = {}
    factors = {'cache_k': 3.433,
     'norm_ffn': 3.001,
     'conv_ln_g': 3.802,
     'conv_ln_b': 4.125,
     'kv_norm': 8.21,
     'w_q': 2.948,
     'final_norm': 8.446,
     'conv_b_pw2': 4.222}
    for name, (base, spread) in spreads.items():
        noise = np.random.default_rng([zlib.crc32(name.encode()), seed]).standard_normal(out[name].shape)
        drawn = base * np.exp(spread * noise) if base else spread * noise
        out[name] = __import__('jax').numpy.asarray(drawn.astype(out[name].dtype))
    for name, factor in factors.items():
        out[name] = (out[name] * factor).astype(out[name].dtype)
    return out
```

```python
from contextlib import ExitStack

import numpy as np

import concourse.bass as bass
from concourse import mybir

F32 = mybir.dt.float32
F32R = mybir.dt.float32r
I32 = mybir.dt.int32
ALU = mybir.AluOpType
ACT = mybir.ActivationFunctionType
ds = bass.ds

P = 128
D = 1024
KC = D // P
SEQ = 1024
NB, NQ = 8, 4
NS = NB * NQ
T = SEQ + NS
NTG = 3
TG = T // NTG
PT2 = SEQ - 2 * TG
FC = 2816 // P
NG = FC // 2
H, DH = 16, 64
W = 31
PAD = W - 1
PE_TAPS = 7
LATE_PE_TAPS = (8, 16)
LOOP_CHUNKS = KC - 2
CONV_OPS = 2 * (W - PE_TAPS)


def pe_taps(c):
    return LATE_PE_TAPS[c - LOOP_CHUNKS] if isinstance(c, int) and c >= LOOP_CHUNKS else PE_TAPS


def conv_ops_before(c):
    late = range(LOOP_CHUNKS, c) if isinstance(c, int) else ()
    return c * CONV_OPS - 2 * sum(pe_taps(i) - PE_TAPS for i in late)
SLOT = PAD + NQ
RMS_EPS, LN_EPS = 1e-6, 1e-5
RAW, RING = 2, 4
QT = 512
CLIP = 30.0
EXP_CLIP = 2.0 ** 60
DEC_SPLIT = 6
NZ = 6
LEAD = 6
LN_EXP_SET = 6

PARAMS = [("g_mix0", 8), ("g_ffn0", 8), ("g_kv", 8), ("g_mix1", 8), ("g_ffn1", 8), ("g_final", 8),
          ("b_pw1", 16), ("b_dw", 8), ("ln_g", 8), ("ln_b", 8), ("b_pw2", 8), ("w_dw", 8 * W)]
NPAR = sum(n for _, n in PARAMS)

U_PW1 = 0
U_PW2 = U_PW1 + 16
U_FFN0 = U_PW2 + 8
U_K = U_FFN0 + 3 * FC
U_V = U_K + 8
U_Q = U_V + 8
U_O = U_Q + 8
U_FFN1 = U_O + 8
UNITS = U_FFN1 + 3 * FC
UNITS_CONV = U_PW2
UNITS_ATT = U_O + 2
assert UNITS % 4 == 0 and UNITS_CONV % 4 == 0 and UNITS_ATT % 4 == 0


def attention_steps():
    steps = []
    for e in range(2):
        for qt in range(SEQ // QT):
            top = (qt + 1) * (QT // P) - 1
            for b in range(top, -1, -1):
                c0 = max(0, P * (b - qt * (QT // P)))
                steps.append(dict(e=e, qt=qt, b=b, c0=c0, diag=b >= qt * (QT // P), first=b == top, last=b == 0,
                                  carry0=min(QT, c0 + P) if b >= qt * (QT // P) else 0))
    masks = carries = blocks = 0
    for s in steps:
        masks += s["diag"]
        carries += not (s["first"] or s["last"])
        blocks += s["diag"] and not s["last"]
        s["masks"], s["carries"], s["blocks"] = masks, carries, blocks
    return steps


STEPS = attention_steps()
NSTEP = len(STEPS)
NMASK, NCARRY = STEPS[-1]["masks"], STEPS[-1]["carries"]
NBLOCK = STEPS[-1]["blocks"]
HSTEP = NSTEP // 2
QSTEP = QT // P


def carries_before(t, back):
    t -= back
    return STEPS[t]["carries"] if t >= 0 else STEPS[t]["carries"] - NCARRY


def attention_slots(eng, stages):
    for slot in range(-LEAD, 0):
        for f, lead in stages:
            if slot + lead >= 0:
                f(0, slot + lead)
    with eng.Fori(0, H // 2 - 1) as it:
        for slot in range(NSTEP):
            for f, lead in stages:
                t = slot + lead
                f(it if t < NSTEP else it + 1, t % NSTEP)
    for slot in range(NSTEP):
        for f, lead in stages:
            if slot + lead < NSTEP:
                f(H // 2 - 1, slot + lead)


def layer_jobs(wide):
    return [(u, tg) for tg in range(NTG) for u in range(wide)] + \
           [(u, tg) for u in range(wide, KC) for tg in range(NTG)]


PAIR_FIRST, FOUR_FIRST = layer_jobs(2), layer_jobs(4)
PAIR_LAST = [(u, tg) for u in range(KC - 2) for tg in range(NTG)] + \
            [(u, tg) for tg in range(NTG) for u in (KC - 2, KC - 1)]
GROUP_JOBS = [(cc, tg) for cc in range(2) for tg in range(NTG)]
FIRST_GROUP_JOBS = [(cc, tg) for tg in range(NTG) for cc in range(2)]


def tiles_until(jobs, u, tg=NTG - 1):
    return jobs.index((u, tg)) + 1


def wait_alone(eng, semaphore, value):
    eng.wait_ge(semaphore, value)
    eng.sem_inc(PASSED[0], 1)


PASSED = [None]


def build(nc, x_t, params, wstream, conv_state, cache_kt, cache_v, page_table, bias_row, bias_dec,
          y_t, u_tail, us_tail, k_t, v_nat, k_scr, q_scr):
    ctx = ExitStack()

    def sem(name):
        return ctx.enter_context(nc.semaphore(name))

    def sb(name, shape, dt=F32, stack=None):
        return (stack or ctx).enter_context(nc.sbuf_tensor(name, shape, dt))

    PASSED[0] = sem("waits_passed")

    x = sb("x", [P, KC, T])
    xh = sb("xh", [P, KC, T], F32R)
    xl = sb("xl", [P, KC, T], F32R)
    w_raw = sb("w_raw", [P, RAW, KC * P])
    wh = sb("wh", [P, RING, KC * P], F32R)
    wl = sb("wl", [P, RING, KC * P], F32R)
    par = sb("par", [P, NPAR])
    eps = sb("eps", [P, 2])
    mean_w = sb("mean_w", [P, P])
    ident = sb("ident", [P, P])
    neg_tri = sb("neg_tri", [P, P])
    neg_one = sb("neg_one", [P, P])
    neg_tri_r = sb("neg_tri_r", [P, P], F32R)
    rstd = sb("rstd", [P, T])
    ssq = sb("ssq", [P, T])
    sq = sb("sq", [P, 2, TG])
    lnv = sb("lnv", [P, TG])
    xg = sb("xg", [P, 3, TG])
    q_dec = sb("q_dec", [P, KC, NB, 2 * NQ])
    with ExitStack() as r:
        cv = sb("cv", [P, KC, T], F32, r)
        us = sb("us", [P, KC, NB, SLOT], F32, r)
        ub = sb("ub", [P, PAD + SEQ], F32, r)
    with ExitStack() as r:
        hh = sb("hh", [P, 4, T], F32R, r)
        hl = sb("hl", [P, 4, T], F32R, r)
        sg = sb("sg", [P, 2, TG], F32, r)
        hf = sb("hf", [P, 2, TG], F32, r)
    with ExitStack() as r:
        stage = sb("stage", [P, 2, T], F32, r)
        stage_h = sb("stage_h", [P, 2, SEQ], F32R, r)
        stage_l = sb("stage_l", [P, 2, SEQ], F32R, r)
        vn = sb("vn", [P, 6, QT], F32, r)
    with ExitStack() as r:
        s_sb = sb("s_sb", [P, 3, QT], F32, r)
        sh_sb = sb("sh_sb", [P, 3, QT], F32R, r)
        sl_sb = sb("sl_sb", [P, 3, QT], F32R, r)
        a_sb = sb("a_sb", [P, 3, QT], F32, r)
        sb("gap", [P, 2 * (T - SEQ)], F32, r)
        k_sb = sb("k_sb", [P, 2, SEQ], F32R, r)
        v_sb = sb("v_sb", [P, 2, SEQ // P, DH], F32, r)
        qh_sb = sb("qh_sb", [P, SEQ], F32R, r)
        ql_sb = sb("ql_sb", [DH, SEQ], F32R, r)
        b_sb = sb("b_sb", [P, 2], F32, r)
    with ExitStack() as r:
        kp = sb("kp", [P, 4, KC, P], F32, r)
        vp = sb("vp", [P, 4, D], F32, r)
        kn = sb("kn", [P, KC, NS], F32, r)
        vnew = sb("vnew", [NS, D], F32, r)
        b_dec = sb("b_dec", [1, QT], F32, r)
        one_row = sb("one_row", [1, P], F32, r)
        pages = sb("pages", [1, 2 * NB], I32, r)
        ds_sb = sb("ds_sb", [P, 3, QT], F32, r)
    da_sb = ds_sb

    def halves(tile):
        return [tile[:, i * QT:(i + 1) * QT] for i in range(2)]

    carry = halves(ssq) + halves(xg[:].rearrange("p a t -> p (a t)"))
    soft = halves(rstd)

    ubs = [ub, ssq]
    diag_memory = (xg[:].rearrange("p a t -> p (a t)"), rstd)

    def diag(k):
        return diag_memory[k // 8][:, k % 8 * P:(k % 8 + 1) * P]

    banks = [ctx.enter_context(nc.psum_tensor(f"bank{i}", [P, 512], F32)) for i in range(8)]
    A, B, DN = banks[0:3], banks[3:6], banks[6:8]
    Z = banks[0:NZ]

    off = {}
    o = 0
    for name, n in PARAMS:
        off[name] = o
        o += n

    def pcol(name, c):
        if isinstance(c, int):
            return par[:, off[name] + c:off[name] + c + 1]
        return par[:, ds(c + off[name], 1)]

    def tgs(tg):
        return slice(tg * TG, (tg + 1) * TG)

    w_in = [sem(f"w_in{i}") for i in range(RAW)]
    w_hi = sem("w_hi")
    w_split = sem("w_split")
    w_done = sem("w_done")
    x_in = [sem(f"x_in{tg}") for tg in range(NTG)]
    par_in = sem("par_in")
    us_in = sem("us_in")
    consts = sem("consts")
    const_steps = sem("const_steps")

    class Norm:
        def __init__(self, name):
            self.sq = sem(name + "_sq")
            self.ssq = sem(name + "_ssq")
            self.ms = sem(name + "_ms")
            self.ln = sem(name + "_ln")
            self.rstd = sem(name + "_rstd")
            self.xg = sem(name + "_xg")
            self.hi = sem(name + "_hi")
            self.ready = sem(name + "_ready")

    n_mix0, n_ffn0, n_kv, n_ffn1, n_fin = (Norm(n) for n in ("mix0", "ffn0", "kv", "ffn1", "fin"))

    class Requant:
        def __init__(self, name):
            self.rstd = None
            self.xg, self.hi, self.ready = sem(name + "_xg"), sem(name + "_hi"), sem(name + "_ready")

    n_mix1 = Requant("mix1")

    class Glu:
        done = sem("glu_done")
        sig = sem("glu_sig")
        out = sem("glu_out")
        diag = sem("conv_diag")
        taps = sem("conv_taps")
        init = sem("conv_init")
        conv = sem("conv_step")
        saved = [sem("conv_saved0"), sem("conv_saved1")]
        dec_saved = sem("conv_dec_saved")
        dec = sem("conv_dec")
        mean = sem("ln_mean")
        cen = sem("ln_cen")
        sq = sem("ln_sq")
        sqr = sem("ln_sqr")
        ln = sem("ln_ln")
        rstd = sem("ln_rstd")
        y = sem("ln_y")
        act = sem("ln_act")
        hi = sem("ln_hi")
        ready = sem("ln_ready")

    class Lin:
        done = sem("lin_done")
        out = sem("lin_out")

        def __init__(self, index):
            self.base = index * NTG * KC

    l_pw2, l_k, l_v, l_q, l_o = (Lin(i) for i in range(5))
    k_stored = [sem("k_stored0"), sem("k_stored1")]
    v_turn = sem("v_turn")
    v_copy = sem("v_copy")
    v_stored = [sem(f"v_stored{i}") for i in range(6)]
    q_stored = [sem("q_stored0"), sem("q_stored1")]
    kq_lo = sem("kq_lo")
    q_zero = sem("q_zero")
    ub_pad = sem("ub_pad")
    q_bd = sem("q_bd")

    class Ffn:
        up = sem("ffn_up")
        silu = sem("ffn_silu")
        mul = sem("ffn_mul")
        hi = sem("ffn_hi")
        lo = sem("ffn_lo")
        down = sem("ffn_down")
        add = sem("ffn_add")

        def __init__(self, index):
            self.hidden = index * FC * NTG
            self.outs = index * NG * KC * NTG

    f0, f1 = Ffn(0), Ffn(1)

    class Att:
        k_in = [sem("k_in0"), sem("k_in1")]
        q_in = [sem("q_in0"), sem("q_in1")]
        v_in = [sem("v_in0"), sem("v_in1")]
        z = sem("z_done")
        exp = sem("z_exp")
        clip = sem("z_clipped")
        ln = sem("z_ln")
        s = sem("s_done")
        s_mask = sem("s_mask")
        sh = [sem("s_hi_even"), sem("s_hi_odd")]
        sl = sem("s_lo")
        carry = sem("carry_done")
        block = sem("carry_block")
        cum = sem("cum_done")
        a = sem("a_done")
        a_mask = sem("a_mask")
        av = sem("av_done")
        o_hi = sem("o_hi")
        o_lo = sem("o_lo")

    class Dec:
        k_in = [sem(f"kp_in{i}") for i in range(4)]
        v_in = [sem(f"vp_in{i}") for i in range(4)]
        new_in = sem("dec_new_in")
        page_in = sem("dec_page_in")
        one = sem("dec_one")
        kz = sem("dec_kz")
        z = sem("dec_z")
        clip = sem("dec_clip")
        exp = sem("dec_exp")
        ln = sem("dec_ln")
        s = sem("dec_s")
        s_mask = sem("dec_s_mask")
        cum = sem("dec_cum")
        a = sem("dec_a")
        a_mask = sem("dec_a_mask")
        pv = sem("dec_pv")
        o_hi = sem("dec_o_hi")
        o_lo = sem("dec_o_lo")

    y_out = sem("y_out")

    block = ctx.enter_context(nc.Block())

    @block.sync
    def _(sp):
        def load_units(first, last):
            with sp.Fori(0, (last - first) // 4) as it:
                for s in range(4):
                    u = it * 4 + (first + s)
                    wait_alone(sp, w_split, u + 1)
                    sp.dma_start(w_raw[:, s % RAW], wstream[ds(u, 1)].rearrange("a p n -> (a p) n"))\
                      .then_inc(w_in[s % RAW], 16)

        load_units(0, UNITS_ATT)
        for n in range(2):
            sp.wait_ge(k_stored[n], 5 * 16 * (KC // 2))
        for n in range(6):
            sp.wait_ge(v_stored[n], 16 * (3 * KC // 6))

        def load_queries(it, e, qt):
            cols = slice(qt * QT, (qt + 1) * QT)
            q = q_scr[ds(it * 2 + e, 1), :, :, cols].rearrange("a s d t -> (a s) d t")
            for out, part in ((qh_sb[0:DH, cols], 0), (qh_sb[DH:P, cols], 0), (ql_sb[:, cols], 1)):
                sp.dma_start(out.bitcast(F32), q[part]).then_inc(Att.q_in[qt], 16)

        def load_pair(it):
            for e in range(2):
                head = it * NSTEP + HSTEP * e
                wait_alone(sp, Att.z, head + HSTEP)
                sp.dma_start(k_sb[:, e].bitcast(F32), k_scr[ds(it * 2 + e, 1)].rearrange("a s d t -> (a s d) t"))\
                  .then_inc(Att.k_in[e], 16)
                wait_alone(sp, Att.z, head + HSTEP + QSTEP)
                load_queries(it, e, 0)
                wait_alone(sp, Att.av, head + HSTEP)
                sp.dma_start(b_sb[:, e:e + 1], bias_row[ds(it * 2 + e, 1), :].rearrange("a p -> p a"))\
                  .then_inc(Att.v_in[e], 16)
                sp.dma_start(v_sb[:, e], v_nat[0:SEQ, ds(it * P + DH * e, DH)].rearrange("(b p) d -> p b d", p=P))\
                  .then_inc(Att.v_in[e], 16)
                wait_alone(sp, Att.z, head + NSTEP)
                load_queries(it, e, 1)
        sp.wait_ge(q_stored[0], 4 * 16)
        load_pair(0)
        for n in range(2):
            sp.wait_ge(q_stored[n], 4 * 16 * (KC // 2))
        with sp.Fori(0, H // 2 - 1) as it:
            load_pair(it + 1)
        sp.wait_ge(Att.o_lo, 2 + 2 * H)
        sp.dma_start(pages[:], page_table).then_inc(Dec.page_in, 16)
        sp.dma_start(kn[:], k_t[:, SEQ:T].rearrange("(c p) t -> p c t", p=P)).then_inc(Dec.new_in, 16)
        sp.dma_start(vnew[:], v_nat[SEQ:T, :]).then_inc(Dec.new_in, 16)
        sp.dma_start(b_dec[:], bias_dec).then_inc(Dec.new_in, 16)
        sp.wait_ge(Dec.page_in, 16)
        for n in range(2 * NB):
            page = sp.value_load(pages[0:1, n:n + 1], min_val=0, max_val=cache_v.shape[0] - 1)
            sp.wait_ge(Dec.kz, n + 1)
            sp.dma_start(kp[:, n % 4], cache_kt[ds(page, 1)].rearrange("a p c k -> (a p) c k"))\
              .then_inc(Dec.k_in[n % 4], 16)
        for n in range(2 * NB):
            page = sp.value_load(pages[0:1, n:n + 1], min_val=0, max_val=cache_v.shape[0] - 1)
            sp.wait_ge(Dec.pv, n + 1)
            sp.dma_start(vp[:, n % 4], cache_v[ds(page, 1)].rearrange("a k n -> (a k) n"))\
              .then_inc(Dec.v_in[n % 4], 16)
        load_units(UNITS_ATT, UNITS)

    @block.gpsimd
    def _(pool):
        pool.sem_inc(w_split, RAW)
        pool.sem_inc(Att.carry, 2)
        pool.memset(eps[:, 0:1], RMS_EPS).then_inc(consts, 1)
        pool.memset(eps[:, 1:2], LN_EPS).then_inc(consts, 1)
        pool.memset(mean_w[:], 1.0 / D).then_inc(consts, 1)
        pool.memset(neg_one[:], -1.0).then_inc(consts, 1)
        pool.memset(ident[:], 0.0).then_inc(const_steps, 1)
        pool.memset(neg_tri[:], -1.0).then_inc(const_steps, 1)
        pool.wait_ge(const_steps, 2)
        pool.affine_select(out=ident[:], in_=ident[:], compare_op=ALU.not_equal, fill=1.0, base=0,
                           pattern=[[-1, P]], channel_multiplier=1).then_inc(consts, 1)
        pool.affine_select(out=neg_tri[:], in_=neg_tri[:], compare_op=ALU.is_ge, fill=0.0, base=0,
                           pattern=[[-1, P]], channel_multiplier=1).then_inc(consts, 1)
        pool.memset(ub[:, 0:PAD], 0.0).then_inc(consts, 1)

        def split_units(first, last):
            with pool.Fori(0, (last - first) // 4) as it:
                for s in range(4):
                    u = it * 4 + (first + s)
                    q, r = divmod(first + s, RAW)
                    pool.wait_ge(w_in[r], (it * (4 // RAW) + (q + 1)) * 16)
                    wait_alone(pool, w_done, u + 2)
                    pool.tensor_copy(wh[:, s], w_raw[:, s % RAW]).then_inc(w_hi, 1)
                    pool.wait_ge(w_hi, u + 1)
                    pool.tensor_tensor(wl[:, s], w_raw[:, s % RAW], wh[:, s].bitcast(F32), ALU.subtract)\
                        .then_inc(w_split, 1)

        split_units(0, UNITS_CONV)

        pool.wait_ge(us_in, 16)
        w_all = par[:, off["w_dw"]:off["w_dw"] + KC * W].rearrange("p (c k) -> p c k", k=W)
        taps = q_dec[:].rearrange("p c b q -> p (c b q)").rearrange("p (n c b q) -> p n c b q", n=2, c=KC, b=NB)

        def decode_conv(part, chunks):
            count = part * 2 * W
            shape = [P, chunks.stop - chunks.start, NB, NQ]
            acc = cv[:, chunks, SEQ:T].rearrange("p c (b q) -> p c b q", q=NQ)

            def per_chunk(cols):
                return cols.unsqueeze(2).unsqueeze(3).to_broadcast(shape)

            bias = per_chunk(par[:, off["b_dw"] + chunks.start:off["b_dw"] + chunks.stop])
            pool.wait_ge(Glu.out, 3 + NTG * chunks.stop)
            for k in range(W):
                tap = taps[:, k % 2, chunks]
                if k >= 2:
                    pool.wait_ge(Glu.dec, count + 2 * k - 2)
                pool.tensor_tensor(tap, us[:, chunks, :, k:k + NQ], per_chunk(w_all[:, chunks, k]), ALU.mult)\
                    .then_inc(Glu.dec, 1)
                pool.wait_ge(Glu.dec, count + 2 * k + 1)
                pool.tensor_tensor(acc, tap, bias if k == 0 else acc, ALU.add).then_inc(Glu.dec, 1)

        decode_conv(0, slice(0, DEC_SPLIT))
        decode_conv(1, slice(DEC_SPLIT, KC))
        pool.wait_ge(Glu.dec, 4 * W)
        pool.memset(q_dec[:], 0.0).then_inc(q_zero, 1)

        split_units(UNITS_CONV, UNITS_ATT)

        def strict_mask(tile):
            return pool.affine_select(out=tile, in_=tile, compare_op=ALU.is_ge, fill=0.0, base=-1,
                                      pattern=[[1, P]], channel_multiplier=-1)

        def att_s_mask(it, t):
            s, g = STEPS[t], it * NSTEP + t
            if s["diag"]:
                wait_alone(pool, Att.s, g + 3)
                strict_mask(s_sb[:, t % 3, s["c0"]:s["c0"] + P]).then_inc(Att.s_mask, 1)

        def att_carry(it, t):
            s, g = STEPS[t], it * NSTEP + t
            if s["first"] or s["last"]:
                return
            cols = slice(s["carry0"], QT)
            pool.wait_ge(Att.cum, g + 1)
            pool.wait_ge(Att.s, g + 3)
            pool.wait_ge(Att.block, it * NBLOCK + STEPS[t - 1]["blocks"])
            pool.wait_ge(Att.carry, it * NCARRY + (STEPS[t - 1]["carries"] + 2))
            pool.tensor_tensor(carry[(t + 1) % 4][:, cols], carry[t % 4][:, cols], s_sb[:, t % 3, cols], ALU.add)\
                .then_inc(Att.carry, 1)

        def att_a_mask(it, t):
            s, g = STEPS[t], it * NSTEP + t
            if s["diag"]:
                wait_alone(pool, Att.a, g + 1 + NZ)
                strict_mask(a_sb[:, t % 3, s["c0"]:s["c0"] + P]).then_inc(Att.a_mask, 1)

        attention_slots(pool, ((att_a_mask, 1), (att_carry, 4), (att_s_mask, 5)))

        pool.wait_ge(Att.o_lo, 2 + 2 * H)
        pool.memset(one_row[:], 1.0).then_inc(Dec.one, 1)

        def dec_mask(done, tile):
            v = tile.rearrange("p (c b e q) -> p c b e q", c=KC, b=NB, e=2)
            for n, (base, pat, mul) in enumerate((
                    (0, [[-NQ, NB], [0, 2], [0, NQ]], 1),
                    (-1, [[NQ, NB], [0, 2], [1, NQ]], -1))):
                for c in range(KC):
                    if n:
                        pool.wait_ge(done, c + 1)
                    pool.affine_select(out=v[:, c], in_=v[:, c], compare_op=ALU.is_ge, fill=0.0, base=base,
                                       pattern=pat, channel_multiplier=mul).then_inc(done, 1)

        pool.wait_ge(Dec.s, 1)
        dec_mask(Dec.s_mask, ds_sb[0:NS, 2, :])
        pool.wait_ge(Dec.a, 1)
        dec_mask(Dec.a_mask, da_sb[0:NS, 2, :])

        split_units(UNITS_ATT, UNITS)

    @block.scalar
    def _(act):
        def table(set_id):
            act.add_instruction(mybir.InstLoadActFuncSet(name=nc.get_next_instruction_name(),
                                                         act_func_set_id=set_id, ins=[], outs=[]))

        for tg in range(NTG):
            act.dma_start(x[:, :, tgs(tg)], x_t[:, tgs(tg)].rearrange("(c p) t -> p c t", p=P)).then_inc(x_in[tg], 16)
        act.dma_start(par[:], params).then_inc(par_in, 16)
        act.dma_start(us[:], conv_state).then_inc(us_in, 16)
        act.sem_inc(Glu.saved[0], 16)
        act.sem_inc(Glu.saved[1], 16)
        act.sem_inc(Ffn.hi, 2)
        act.sem_inc(Att.a, NZ)

        def square(n, j, tile):
            act.wait_ge(n.ssq, j + 1)
            act.activation(sq[:, j % 2], tile, ACT.Square).then_inc(n.sq, 1)

        def inv_rms(n, tg, bank):
            if tg:
                act.wait_ge(n.rstd, tg)
            act.wait_ge(n.ms, tg + 1)
            act.activation(lnv[:], bank[:, 0:TG], ACT.Ln, bias=eps[:, 0:1]).then_inc(n.ln, 1)
            act.wait_ge(n.ln, tg + 1)
            act.activation(rstd[:, tgs(tg)], lnv[:], ACT.Exp, scale=-0.5).then_inc(n.rstd, 1)

        def split_norm(n, tg):
            for c in range(KC):
                j = tg * KC + c
                act.wait_ge(n.xg, j + 1)
                act.activation(xh[:, c, tgs(tg)], xg[:, j % 3], ACT.Copy).then_inc(n.hi, 1)

        def norm(n, bank_of):
            table(LN_EXP_SET)
            for tg in range(NTG):
                inv_rms(n, tg, bank_of(tg))
                split_norm(n, tg)

        act.wait_ge(consts, 7)
        act.activation(neg_tri_r[:], neg_tri[:], ACT.Copy).then_inc(consts, 1)
        for tg in range(NTG):
            act.wait_ge(x_in[tg], 16)
            for c in range(KC):
                square(n_mix0, tg * KC + c, x[:, c, tgs(tg)])
        norm(n_mix0, lambda tg: A[tg])

        act.wait_ge(par_in, 16)
        act.wait_ge(n_mix0.ready, NTG * KC)
        def conv_chunk(it, u):
            c = it * 2 + u
            taps = pe_taps(c)
            wait_alone(act, Glu.taps, c + 1)
            for k in range(taps):
                mm = act.activation(diag(k), ident[:], ACT.Copy, scale=pcol("w_dw", c * W + (W - taps + k)))
            mm.then_inc(Glu.diag, 1)
            for tg in range(NTG):
                j = it * (2 * NTG) + (u * NTG + tg)
                act.wait_ge(Glu.done, j + 1)
                wait_alone(act, Glu.out, j + 3)
                act.activation(sq[:, tg % 2], B[tg][:, 0:TG], ACT.Sigmoid, bias=pcol("b_pw1", c + KC))\
                   .then_inc(Glu.sig, 1)
            wait_alone(act, Glu.out, it * (2 * NTG) + (u * NTG + 3 + NTG))
            act.dma_start(u_tail[ds(c, 1)].rearrange("a p n -> (a p) n"), ubs[u][:, SEQ:SEQ + PAD])\
               .then_inc(Glu.saved[u], 16)
            wait_alone(act, Glu.taps, c + 2)
            for h in range(2):
                ins = act.activation(cv[:, ds(c, 1), h * QT:(h + 1) * QT].rearrange("p a t -> p (a t)"), DN[h][:],
                                     ACT.Identity, bias=pcol("b_dw", c))
            ins.then_inc(Glu.init, 1)

        with act.Fori(0, LOOP_CHUNKS // 2) as it:
            conv_chunk(it, 0)
            conv_chunk(it, 1)
        conv_chunk(LOOP_CHUNKS // 2, 0)
        conv_chunk(LOOP_CHUNKS // 2, 1)
        act.dma_start(us_tail, us[:]).then_inc(Glu.dec_saved, 16)

        def ln_squares(tg):
            for c in range(KC):
                j = tg * KC + c
                act.wait_ge(Glu.cen, j + 1)
                act.wait_ge(Glu.sqr, j + 1)
                act.activation(sq[:, j % 2], cv[:, c, tgs(tg)], ACT.Square).then_inc(Glu.sq, 1)

        def ln_tail(tg):
            table(LN_EXP_SET)
            act.wait_ge(Glu.sqr, 2 + (tg + 1) * KC)
            if tg:
                act.wait_ge(Glu.rstd, tg)
            act.activation(lnv[:], DN[tg % 2][:, 0:TG], ACT.Ln, bias=eps[:, 1:2]).then_inc(Glu.ln, 1)
            act.wait_ge(Glu.ln, tg + 1)
            act.activation(rstd[:, tgs(tg)], lnv[:], ACT.Exp, scale=-0.5).then_inc(Glu.rstd, 1)
            for c in range(KC):
                j = tg * KC + c
                act.wait_ge(Glu.y, j + 1)
                if j >= 3:
                    act.wait_ge(Glu.ready, j - 2)
                act.activation(xg[:, j % 3], cv[:, c, tgs(tg)], ACT.Silu, bias=pcol("ln_b", c),
                               scale=pcol("ln_g", c)).then_inc(Glu.act, 1)
                act.wait_ge(Glu.act, j + 1)
                act.activation(xh[:, c, tgs(tg)], xg[:, j % 3], ACT.Copy).then_inc(Glu.hi, 1)

        ln_squares(0)
        ln_squares(1)
        ln_tail(0)
        ln_squares(2)
        ln_tail(1)
        ln_tail(2)

        def residual_squares(l, n):
            for j, (u, tg) in enumerate(FOUR_FIRST):
                act.wait_ge(l.out, l.base + j + 7)
                square(n, j, x[:, u, tgs(tg)])

        residual_squares(l_pw2, n_ffn0)
        norm(n_ffn0, lambda tg: DN[tg % 2])

        def ffn(f, n_next):
            def tile(it, jj, cc, parity, tg):
                j = it * 6 + (f.hidden + jj)
                act.wait_ge(f.up, j + 1)
                act.wait_ge(f.mul, j + 2)
                act.activation(sg[:, jj % 2], A[jj % 3][:, 0:TG], ACT.Silu).then_inc(f.silu, 1)
                act.wait_ge(f.mul, j + 4)
                act.activation(hh[:, 2 * parity + cc, tgs(tg)], hf[:, jj % 2], ACT.Copy).then_inc(f.hi, 1)

            def group(it, parity, jobs=GROUP_JOBS):
                for jj, (cc, tg) in enumerate(jobs):
                    tile(it, jj, cc, parity, tg)

            group(0, 0, FIRST_GROUP_JOBS)
            with act.Fori(0, NG // 2) as it:
                act.wait_ge(f.down, it * 48 + (f.outs + 1))
                group(it * 2 + 1, 1)
                act.wait_ge(f.down, it * 48 + (f.outs + 25))
                group(it * 2 + 2, 0)
            for tg in range(NTG):
                for c in range(KC):
                    j = tg * KC + c
                    act.wait_ge(f.add, f.outs + 2 + 24 * (NG - 1) + j + 1)
                    square(n_next, j, x[:, c, tgs(tg)])

        act.wait_ge(Glu.dec_saved, 16)
        for n in range(2):
            act.wait_ge(Glu.saved[n], 16 * (KC // 2 + 1))
        ffn(f0, n_kv)
        norm(n_kv, lambda tg: B[tg])

        def project_out(l, out, scr, stored, scale):
            base = 0 if l is l_k else NTG * KC
            per_chunk = (4 + (out is not None)) * 16

            def store(c):
                act.wait_ge(l.out, l.base + 6 + tiles_until(PAIR_FIRST, c))
                act.wait_ge(kq_lo, base + tiles_until(PAIR_FIRST, c))
                if out is not None:
                    act.dma_start(out[c * P:(c + 1) * P, :], stage[:, c % 2]).then_inc(stored[c % 2], 16)
                for e in range(2):
                    for i, part in enumerate((stage_h, stage_l)):
                        act.dma_start(scr[2 * c + e, i], part[DH * e:DH * (e + 1), c % 2].bitcast(F32))\
                           .then_inc(stored[c % 2], 16)

            for j, (c, tg) in enumerate(PAIR_FIRST):
                if c >= 2 and tg == 0:
                    act.wait_ge(stored[c % 2], per_chunk * (c // 2))
                    if out is None:
                        act.wait_ge(q_bd, 2 * (c - 1))
                n = TG if tg < NTG - 1 else PT2
                act.wait_ge(l.done, l.base + j + 1)
                act.activation(stage[:, c % 2, tgs(tg)], banks[j % 6][:, 0:TG], ACT.Copy, scale=scale)
                act.activation(stage_h[:, c % 2, tg * TG:tg * TG + n], banks[j % 6][:, 0:n], ACT.Copy, scale=scale)\
                   .then_inc(l.out, 1)
                if c and tg == NTG - 1:
                    store(c - 1)
            store(KC - 1)

        def store_values(c):
            for i in range(3):
                n = 3 * c + i
                act.wait_ge(v_copy, n + 3)
                if i < 2:
                    act.dma_start(v_nat[i * QT:(i + 1) * QT, c * P:(c + 1) * P].rearrange("(b p) d -> p b d", p=P),
                                  vn[:, n % 6].rearrange("p (b d) -> p b d", d=P)).then_inc(v_stored[n % 6], 16)
                else:
                    act.dma_start(v_nat[SEQ:T, c * P:(c + 1) * P], vn[0:NS, n % 6, 0:P])\
                       .then_inc(v_stored[n % 6], 16)

        project_out(l_k, k_t, k_scr, k_stored, 1.0)
        for j, (c, tg) in enumerate(PAIR_LAST):
            if tg == 0 and c < 2:
                act.wait_ge(k_stored[c], 5 * 16 * (KC // 2))
            elif tg == 0:
                act.wait_ge(v_turn, 3 * (c - 1))
            act.wait_ge(l_v.done, l_v.base + j + 1)
            act.activation(stage[:, c % 2, tgs(tg)], banks[j % 6][:, 0:TG], ACT.Copy).then_inc(l_v.out, 1)
            if tg == NTG - 1 and 0 < c < KC - 1:
                store_values(c - 1)
        for tg in range(NTG):
            split_norm(n_mix1, tg)
        store_values(KC - 2)
        store_values(KC - 1)
        act.wait_ge(v_turn, 3 * KC)
        project_out(l_q, None, q_scr, q_stored, float(DH) ** -0.5)

        table(LN_EXP_SET)

        def att_exp(it, t):
            s, g = STEPS[t], it * NSTEP + t
            c0, e = s["c0"], s["e"]
            if t % HSTEP == 0:
                act.wait_ge(Att.v_in[e], it * 32 + 32)
            act.wait_ge(Att.z, g + 1 + NSTEP)
            act.wait_ge(Att.s, g + 1)
            act.activation(soft[t % 2][:, c0:QT], Z[t % NZ][:, c0:QT], ACT.Exp, bias=b_sb[:, e:e + 1])\
               .then_inc(Att.exp, 1)

        def att_ln(it, t):
            s, g = STEPS[t], it * NSTEP + t
            tile = soft[t % 2][:, s["c0"]:QT]
            act.wait_ge(Att.clip, g + 1)
            act.activation(tile, tile, ACT.Ln, bias=1.0).then_inc(Att.ln, 1)

        def att_s_hi(it, t):
            s, g = STEPS[t], it * NSTEP + t
            c0 = s["c0"]
            if t % 2:
                return
            if s["diag"]:
                act.wait_ge(Att.s_mask, it * NMASK + s["masks"])
            else:
                act.wait_ge(Att.s, g + 3)
            act.wait_ge(Att.cum, g + 1)
            act.activation(sh_sb[:, t % 3, c0:QT], s_sb[:, t % 3, c0:QT], ACT.Copy).then_inc(Att.sh[0], 1)

        def att_weights(it, t):
            s, g = STEPS[t], it * NSTEP + t
            c0, e = s["c0"], s["e"]
            act.wait_ge(Att.cum, g + 4)
            act.wait_ge(Att.av, g - 2 + NSTEP)
            act.activation(a_sb[:, t % 3, c0:QT], Z[t % NZ][:, c0:QT], ACT.Exp, bias=b_sb[:, e:e + 1])\
               .then_inc(Att.a, 1)

        def att_out(it, t):
            s, g = STEPS[t], it * NSTEP + t
            if s["last"]:
                rows = slice(DH * s["e"], DH * s["e"] + DH)
                cols = slice(s["qt"] * QT, (s["qt"] + 1) * QT)
                wait_alone(act, Att.av, g + 1 + NSTEP)
                act.activation(xh[rows, ds(it, 1), cols], DN[s["qt"]][rows, :], ACT.Copy).then_inc(Att.o_hi, 1)

        attention_slots(act, ((att_weights, 1), (att_s_hi, 4), (att_ln, 5), (att_exp, 6), (att_out, 0)))

        for n, (i, rows) in enumerate(((2, NS), (1, P), (0, P))):
            act.wait_ge(Dec.clip, n + 1)
            act.activation(ds_sb[0:rows, i], ds_sb[0:rows, i], ACT.Exp).then_inc(Dec.exp, 1)
            act.wait_ge(Dec.exp, n + 1)
            act.activation(ds_sb[0:rows, i], ds_sb[0:rows, i], ACT.Ln, bias=1.0).then_inc(Dec.ln, 1)
        for n, (i, rows) in enumerate(((2, NS), (1, P), (0, P))):
            act.wait_ge(Dec.cum, 3)
            act.activation(da_sb[0:rows, i], Z[i][0:rows, :], ACT.Exp).then_inc(Dec.a, 1)
        act.wait_ge(Dec.pv, 4 + 2 * NB)
        for e in range(2):
            rows = slice(DH * e, DH * e + DH)
            act.activation(xh[rows, :, SEQ:T].rearrange("p c (b q) -> p c b q", q=NQ),
                           DN[0][rows, :].rearrange("p (c b e q) -> p c b e q", c=KC, b=NB, e=2)[:, :, :, e],
                           ACT.Copy).then_inc(Dec.o_hi, 1)

        residual_squares(l_o, n_ffn1)
        norm(n_ffn1, lambda tg: DN[tg % 2])
        ffn(f1, n_fin)

        table(LN_EXP_SET)
        for tg in range(NTG):
            inv_rms(n_fin, tg, B[tg])
        for tg in range(NTG):
            for c in range(KC):
                act.wait_ge(n_fin.xg, tg * KC + c + 1)
                act.dma_start(y_t[c * P:(c + 1) * P, tgs(tg)], x[:, c, tgs(tg)]).then_inc(y_out, 16)
        act.wait_ge(y_out, 16 * NTG * KC)

    @block.vector
    def _(v):
        v.sem_inc(Glu.out, 3)
        v.sem_inc(Glu.conv, 2 * CONV_OPS)
        v.sem_inc(Att.s, 2)
        v.sem_inc(Att.sl, 3)
        v.sem_inc(Lin.out, 6)
        v.sem_inc(v_copy, 2)
        v.sem_inc(Att.o_lo, 2)
        v.sem_inc(Ffn.mul, 3)
        v.sem_inc(Ffn.add, 2)
        v.sem_inc(Ffn.lo, 2)

        def clear_ssq(n):
            v.memset(ssq[:], 0.0).then_inc(n.ssq, 2)

        def add_square(n, tg, jj, base=0):
            v.wait_ge(n.sq, base + (jj + 1))
            v.wait_ge(n.ssq, base + (jj + 2))
            v.tensor_tensor(ssq[:, tgs(tg)], ssq[:, tgs(tg)], sq[:, jj % 2], ALU.add).then_inc(n.ssq, 1)

        def normalise(n, g_name, tg):
            if n.rstd is not None:
                v.wait_ge(n.rstd, tg + 1)
            for c in range(KC + 1):
                j = tg * KC + c
                if c < KC:
                    if j >= 3:
                        v.wait_ge(n.ready, j - 2)
                    v.scalar_tensor_tensor(out=xg[:, j % 3], in0=x[:, c, tgs(tg)], scalar=pcol(g_name, c),
                                           in1=rstd[:, tgs(tg)], op0=ALU.mult, op1=ALU.mult).then_inc(n.xg, 1)
                if c:
                    v.wait_ge(n.hi, j)
                    v.tensor_tensor(xl[:, c - 1, tgs(tg)], xg[:, (j - 1) % 3],
                                    xh[:, c - 1, tgs(tg)].bitcast(F32), ALU.subtract).then_inc(n.ready, 1)

        clear_ssq(n_mix0)
        for tg in range(NTG):
            for c in range(KC):
                add_square(n_mix0, tg, tg * KC + c)
        v.wait_ge(par_in, 16)
        for tg in range(NTG):
            normalise(n_mix0, "g_mix0", tg)

        v.wait_ge(us_in, 16)
        v.wait_ge(consts, 7)
        v.memset(ssq[:, 0:PAD], 0.0).then_inc(ub_pad, 1)
        v.wait_ge(ub_pad, 1)

        def glu_rows(half, u):
            c = half * 2 + u
            for tg in range(NTG):
                v.wait_ge(Glu.sig, c * NTG + (tg + 1))
                if tg == 0:
                    v.wait_ge(Glu.saved[u], half * 16 + 16)
                    v.wait_ge(Glu.conv, c * CONV_OPS + CONV_OPS)
                n = TG if tg < NTG - 1 else PT2
                ins = v.scalar_tensor_tensor(out=ubs[u][:, PAD + tg * TG:PAD + tg * TG + n], in0=A[tg][:, 0:n],
                                             scalar=pcol("b_pw1", c), in1=sq[:, tg % 2, 0:n],
                                             op0=ALU.add, op1=ALU.mult)
                if tg == NTG - 1:
                    row = us[:, c, :, PAD:SLOT] if isinstance(c, int) else \
                        us[:, ds(c, 1), :, PAD:SLOT].rearrange("p a b q -> p (a b) q")
                    ins = v.scalar_tensor_tensor(
                        out=row, in0=A[tg][:, PT2:TG].rearrange("p (b q) -> p b q", q=NQ), scalar=pcol("b_pw1", c),
                        in1=sq[:, tg % 2, PT2:TG].rearrange("p (b q) -> p b q", q=NQ), op0=ALU.add, op1=ALU.mult)
                ins.then_inc(Glu.out, 1)

        def conv(half, u):
            c = half * 2 + u
            v.wait_ge(Glu.init, c + 1)
            done = conv_ops_before(c) + 2 * CONV_OPS
            for k in range(W - pe_taps(c)):
                tap = par[:, off["w_dw"] + c * W + k:off["w_dw"] + c * W + k + 1] if isinstance(c, int) else \
                    par[:, ds(c * W + (off["w_dw"] + k), 1)]
                for h in range(2):
                    out = cv[:, c, h * QT:(h + 1) * QT] if isinstance(c, int) else \
                        cv[:, ds(c, 1), h * QT:(h + 1) * QT].rearrange("p a t -> p (a t)")
                    if k:
                        v.wait_ge(Glu.conv, done + (2 * k + h - 1))
                    v.scalar_tensor_tensor(out=out, in0=ubs[u][:, h * QT + k:h * QT + k + QT], scalar=tap, in1=out,
                                           op0=ALU.mult, op1=ALU.add).then_inc(Glu.conv, 1)

        glu_rows(0, 0)
        with v.Fori(0, KC // 2 - 1) as it:
            glu_rows(it, 1)
            conv(it, 0)
            glu_rows(it + 1, 0)
            conv(it, 1)
        glu_rows(KC // 2 - 1, 1)
        conv(KC // 2 - 1, 0)
        conv(KC // 2 - 1, 1)

        def ln_centre(tg):
            v.wait_ge(Glu.mean, tg + 1)
            for c in range(KC):
                v.tensor_tensor(cv[:, c, tgs(tg)], cv[:, c, tgs(tg)], A[tg][:, 0:TG], ALU.subtract)\
                 .then_inc(Glu.cen, 1)

        def ln_scale(tg):
            v.wait_ge(Glu.rstd, tg + 1)
            for c in range(KC + 1):
                j = tg * KC + c
                if c < KC:
                    v.tensor_tensor(cv[:, c, tgs(tg)], cv[:, c, tgs(tg)], rstd[:, tgs(tg)], ALU.mult)\
                     .then_inc(Glu.y, 1)
                if c:
                    v.wait_ge(Glu.hi, j)
                    v.tensor_tensor(xl[:, c - 1, tgs(tg)], xg[:, (j - 1) % 3],
                                    xh[:, c - 1, tgs(tg)].bitcast(F32), ALU.subtract).then_inc(Glu.ready, 1)

        ln_centre(0)
        ln_centre(1)
        ln_scale(0)
        ln_centre(2)
        ln_scale(1)
        ln_scale(2)

        def residual(l, n, bias):
            clear_ssq(n)
            for j, (u, tg) in enumerate(FOUR_FIRST):
                xt = x[:, u, tgs(tg)]
                v.wait_ge(l.done, l.base + j + 1)
                if bias:
                    v.scalar_tensor_tensor(out=xt, in0=banks[j % 6][:, 0:TG], scalar=pcol(bias, u),
                                           in1=xt, op0=ALU.add, op1=ALU.add).then_inc(l.out, 1)
                else:
                    v.tensor_tensor(xt, banks[j % 6][:, 0:TG], xt, ALU.add).then_inc(l.out, 1)
                if j:
                    add_square(n, FOUR_FIRST[j - 1][1], j - 1)
            add_square(n, NTG - 1, KC * NTG - 1)

        v.wait_ge(Glu.saved[1], 16 * (KC // 2 + 1))
        residual(l_pw2, n_ffn0, "b_pw2")
        for tg in range(NTG):
            normalise(n_ffn0, "g_ffn0", tg)

        def ffn(f, n_next):
            def group(it, parity, jobs=GROUP_JOBS):
                for jj, (cc, tg) in enumerate(jobs):
                    j = it * 6 + (f.hidden + jj)
                    v.wait_ge(f.silu, j + 1)
                    v.wait_ge(f.lo, j + 1)
                    v.tensor_tensor(hf[:, jj % 2], B[jj % 3][:, 0:TG], sg[:, jj % 2], ALU.mult).then_inc(f.mul, 1)
                    v.wait_ge(f.hi, j + 3)
                    slot = 2 * parity + cc
                    v.tensor_tensor(hl[:, slot, tgs(tg)], hf[:, jj % 2], hh[:, slot, tgs(tg)].bitcast(F32),
                                    ALU.subtract).then_inc(f.lo, 1)

            def down(it):
                for c in range(KC):
                    for tg in range(NTG):
                        n = c * NTG + tg
                        v.wait_ge(f.down, it * 24 + (f.outs + n + 2))
                        v.tensor_tensor(x[:, c, tgs(tg)], DN[n % 2][:, 0:TG], x[:, c, tgs(tg)], ALU.add)\
                         .then_inc(f.add, 1)

            group(0, 0, FIRST_GROUP_JOBS)
            with v.Fori(0, NG // 2) as it:
                group(it * 2 + 1, 1)
                down(it * 2)
                group(it * 2 + 2, 0)
                down(it * 2 + 1)
            clear_ssq(n_next)
            for tg in range(NTG):
                for c in range(KC):
                    j = tg * KC + c
                    v.wait_ge(f.down, f.outs + (NG - 1) * 24 + j + 2)
                    v.tensor_tensor(x[:, c, tgs(tg)], DN[j % 2][:, 0:TG], x[:, c, tgs(tg)], ALU.add)\
                     .then_inc(f.add, 1)
                    if j:
                        add_square(n_next, (j - 1) // KC, j - 1)
            add_square(n_next, NTG - 1, NTG * KC - 1)

        ffn(f0, n_kv)
        for tg in range(NTG):
            normalise(n_kv, "g_kv", tg)

        def stage_lo(l, c, tg):
            n = TG if tg < NTG - 1 else PT2
            v.wait_ge(l.out, l.base + 6 + tiles_until(PAIR_FIRST, c, tg))
            if c >= 2 and tg == 0:
                v.wait_ge(k_stored[c % 2] if l is l_k else q_stored[c % 2], (5 if l is l_k else 4) * 16 * (c // 2))
            cols = slice(tg * TG, tg * TG + n)
            v.tensor_tensor(stage_l[:, c % 2, cols], stage[:, c % 2, cols], stage_h[:, c % 2, cols].bitcast(F32),
                            ALU.subtract).then_inc(kq_lo, 1)

        for c, tg in PAIR_FIRST:
            stage_lo(l_k, c, tg)

        def values(chunks):
            for n in range(3 * chunks.start, 3 * chunks.stop):
                v.wait_ge(v_turn, n + 1)
                if n >= 6:
                    v.wait_ge(v_stored[n % 6], 16 * (n // 6))
                if n % 3 < 2:
                    v.tensor_copy(vn[:, n % 6, :], DN[n % 2][:, :]).then_inc(v_copy, 1)
                else:
                    v.tensor_copy(vn[0:NS, n % 6, 0:P], DN[n % 2][0:NS, 0:P]).then_inc(v_copy, 1)

        values(slice(0, KC - 2))
        for tg in range(NTG):
            v.wait_ge(l_v.done, l_v.base + tiles_until(PAIR_LAST, KC - 1, tg))
            normalise(n_mix1, "g_mix1", tg)
        values(slice(KC - 2, KC))

        v.wait_ge(q_zero, 1)
        for c, tg in PAIR_FIRST:
            stage_lo(l_q, c, tg)
            if tg == NTG - 1:
                for e in range(2):
                    rows = slice(DH * e, DH * e + DH)
                    v.tensor_copy(q_dec[rows, c, :, NQ * e:NQ * e + NQ],
                                  stage[rows, c % 2, SEQ:T].rearrange("p (b q) -> p b q", q=NQ)).then_inc(q_bd, 1)

        def att_clip(it, t):
            s, g = STEPS[t], it * NSTEP + t
            tile = soft[t % 2][:, s["c0"]:QT]
            v.wait_ge(Att.exp, g + 1)
            v.tensor_scalar(tile, tile, EXP_CLIP, None, ALU.min).then_inc(Att.clip, 1)

        def att_max(it, t):
            s, g = STEPS[t], it * NSTEP + t
            c0, e = s["c0"], s["e"]
            v.wait_ge(Att.ln, g + 1)
            v.wait_ge(Att.sl, g + 1)
            v.wait_ge(Att.carry, it * NCARRY + (carries_before(t, 3) + 2))
            v.scalar_tensor_tensor(out=s_sb[:, t % 3, c0:QT], in0=Z[t % NZ][:, c0:QT], scalar=b_sb[:, e:e + 1],
                                   in1=soft[t % 2][:, c0:QT], op0=ALU.add, op1=ALU.max).then_inc(Att.s, 1)

        def att_s_lo(it, t):
            s, g = STEPS[t], it * NSTEP + t
            c0 = s["c0"]
            if t % 2:
                if s["diag"]:
                    v.wait_ge(Att.s_mask, it * NMASK + s["masks"])
                else:
                    v.wait_ge(Att.s, g + 3)
                v.wait_ge(Att.cum, g + 1)
                v.tensor_copy(sh_sb[:, t % 3, c0:QT], s_sb[:, t % 3, c0:QT]).then_inc(Att.sh[1], 1)
            v.wait_ge(Att.sh[t % 2], it * HSTEP + (t // 2 + 1))
            v.tensor_tensor(sl_sb[:, t % 3, c0:QT], s_sb[:, t % 3, c0:QT], sh_sb[:, t % 3, c0:QT].bitcast(F32),
                            ALU.subtract).then_inc(Att.sl, 1)

        def att_block(it, t):
            s, g = STEPS[t], it * NSTEP + t
            if s["diag"] and not s["last"]:
                block = slice(s["c0"], s["c0"] + P)
                v.wait_ge(Att.s_mask, it * NMASK + s["masks"])
                v.wait_ge(Att.cum, g + 1)
                v.tensor_copy(carry[(t + 1) % 4][:, block], s_sb[:, t % 3, block]).then_inc(Att.block, 1)

        def att_out(it, t):
            s = STEPS[t]
            if s["last"]:
                rows = slice(DH * s["e"], DH * s["e"] + DH)
                cols = slice(s["qt"] * QT, (s["qt"] + 1) * QT)
                v.wait_ge(Att.o_hi, it * 4 + (2 * s["e"] + s["qt"] + 1))
                v.tensor_tensor(xl[rows, ds(it, 1), cols].rearrange("p a t -> p (a t)"), DN[s["qt"]][rows, :],
                                xh[rows, ds(it, 1), cols].bitcast(F32).rearrange("p a t -> p (a t)"), ALU.subtract)\
                 .then_inc(Att.o_lo, 1)

        for n in range(2):
            v.wait_ge(q_stored[n], 4 * 16 * (KC // 2))
        attention_slots(v, ((att_s_lo, 4), (att_block, 4), (att_max, 5), (att_clip, 6), (att_out, 0)))

        for n, (i, rows) in enumerate(((2, NS), (1, P), (0, P))):
            v.wait_ge(Dec.z, 1)
            v.tensor_scalar(ds_sb[0:rows, i], Z[i][0:rows, :], CLIP, None, ALU.min).then_inc(Dec.clip, 1)
        for n, (i, rows) in enumerate(((2, NS), (1, P), (0, P))):
            v.wait_ge(Dec.ln, n + 1)
            v.tensor_tensor(ds_sb[0:rows, i], Z[i][0:rows, :], ds_sb[0:rows, i], ALU.max).then_inc(Dec.s, 1)
        v.wait_ge(Dec.o_hi, 2)
        for e in range(2):
            rows = slice(DH * e, DH * e + DH)
            v.tensor_tensor(xl[rows, :, SEQ:T].rearrange("p c (b q) -> p c b q", q=NQ),
                            DN[0][rows, :].rearrange("p (c b e q) -> p c b e q", c=KC, b=NB, e=2)[:, :, :, e],
                            xh[rows, :, SEQ:T].bitcast(F32).rearrange("p c (b q) -> p c b q", q=NQ),
                            ALU.subtract).then_inc(Dec.o_lo, 1)

        v.wait_ge(Att.carry, 2 + H // 2 * NCARRY)
        residual(l_o, n_ffn1, None)
        for tg in range(NTG):
            normalise(n_ffn1, "g_ffn1", tg)
        ffn(f1, n_fin)
        for tg in range(NTG):
            v.wait_ge(n_fin.rstd, tg + 1)
            for c in range(KC):
                v.scalar_tensor_tensor(out=x[:, c, tgs(tg)], in0=x[:, c, tgs(tg)], scalar=pcol("g_final", c),
                                       in1=rstd[:, tgs(tg)], op0=ALU.mult, op1=ALU.mult).then_inc(n_fin.xg, 1)

    @block.tensor
    def _(pe):
        pe.sem_inc(w_done, RING)
        pe.sem_inc(Glu.sqr, 2)
        pe.sem_inc(Glu.taps, 1)
        pe.sem_inc(Att.z, NSTEP)
        pe.sem_inc(Att.av, NSTEP)
        pe.sem_inc(Att.cum, 3)
        pe.sem_inc(Dec.kz, 4)
        pe.sem_inc(Dec.pv, 4)
        pe.sem_inc(Ffn.down, 1)

        def unit_ready(u):
            pe.wait_ge(w_split, u + (1 + RAW))

        def project(slot, tg, bank, done, release, ready=None):
            out = bank[:, 0:TG]
            first = True
            for k in range(KC):
                if ready is not None:
                    pe.wait_ge(ready[0], ready[1] + k + 1)
                w = slice(k * P, (k + 1) * P)
                for i, (a, b) in enumerate(((wh, xh), (wh, xl), (wl, xh))):
                    mm = pe.matmul(out, a[:, slot, w], b[:, k, tgs(tg)], start=(k == 0 and i == 0),
                                   stop=(k == KC - 1 and i == 2))
                    if first and release:
                        mm.then_inc(w_done, 1)
                    first = False
            if done is not None:
                mm.then_inc(done, 1)

        def mean_square(n, tg, bank, count):
            pe.wait_ge(n.ssq, 2 + count)
            pe.matmul(bank[:, 0:TG], mean_w[:], ssq[:, tgs(tg)], start=True, stop=True).then_inc(n.ms, 1)

        def linear(l, first_unit, jobs, ready, after=None):
            for j, (u, tg) in enumerate(jobs):
                if tg == 0:
                    unit_ready(first_unit + u)
                pe.wait_ge(l.out, l.base + j + 1)
                release = j == 0 or jobs[j - 1] == (u - 1, NTG - 1)
                new_group = ready is not None and j == jobs.index((0, tg))
                project((first_unit + u) % RING, tg, banks[j % 6], l.done, release, (ready, tg * KC) if new_group else None)
                if after is not None:
                    after(j)

        pe.wait_ge(consts, 7)
        for tg in range(NTG):
            mean_square(n_mix0, tg, A[tg], (tg + 1) * KC)

        def conv_chunk(it, u):
            unit_ready(it * 4 + 2 * u)
            unit_ready(it * 4 + (2 * u + 1))
            for tg in range(NTG):
                pe.wait_ge(Glu.out, it * (2 * NTG) + (u * NTG + tg + 1))
                ready = (n_mix0.ready, tg * KC) if u == 0 else None
                project(2 * u, tg, A[tg], None, tg == 0, ready)
                project(2 * u + 1, tg, B[tg], Glu.done, tg == NTG - 1)
            taps = pe_taps(it * 2 + u)
            pe.wait_ge(Glu.diag, it * 2 + (u + 1))
            pe.wait_ge(Glu.out, it * (2 * NTG) + (u * NTG + NTG + 3))
            for h in range(2):
                for k in range(taps):
                    at = h * QT + W - taps + k
                    mm = pe.matmul(DN[h][:], diag(k), ubs[u][:, at:at + QT], start=(k == 0), stop=(k == taps - 1))
            mm.then_inc(Glu.taps, 1)

        with pe.Fori(0, LOOP_CHUNKS // 2) as it:
            conv_chunk(it, 0)
            conv_chunk(it, 1)
        conv_chunk(LOOP_CHUNKS // 2, 0)
        conv_chunk(LOOP_CHUNKS // 2, 1)

        pe.wait_ge(Glu.out, 3 + NTG * KC)
        for c in range(KC):
            pe.wait_ge(Glu.conv, conv_ops_before(c + 1) + 2 * CONV_OPS)
            if c == 0 or c == DEC_SPLIT:
                pe.wait_ge(Glu.dec, 2 * W if c == 0 else 4 * W)
            for tg in range(NTG):
                mm = pe.matmul(A[tg][:, 0:TG], mean_w[:], cv[:, c, tgs(tg)], start=(c == 0), stop=(c == KC - 1))
                if c == KC - 1:
                    mm.then_inc(Glu.mean, 1)
        for tg in range(NTG):
            for c in range(KC):
                pe.wait_ge(Glu.sq, tg * KC + c + 1)
                if tg == 2 and c == 0:
                    pe.wait_ge(Glu.ln, 1)
                pe.matmul(DN[tg % 2][:, 0:TG], mean_w[:], sq[:, (tg * KC + c) % 2], start=(c == 0), stop=(c == KC - 1))\
                  .then_inc(Glu.sqr, 1)

        def residual_linear(l, first_unit, ready, n):
            if l is l_pw2:
                pe.wait_ge(Glu.cen, NTG * KC)
            linear(l, first_unit, FOUR_FIRST, ready)
            for tg in range(NTG):
                if tg == 2:
                    pe.wait_ge(n.ln, 1)
                mean_square(n, tg, DN[tg % 2], (KC - 1) * NTG + tg + 1)

        residual_linear(l_pw2, U_PW2, Glu.ready, n_ffn0)

        def ffn(f, first_unit, n_in, n_next):
            def gate_up(it, unit, parity, ready):
                jobs = GROUP_JOBS if ready is None else FIRST_GROUP_JOBS
                for jj, (cc, tg) in enumerate(jobs):
                    if tg == 0:
                        unit_ready(unit + 2 * cc)
                        unit_ready(unit + (2 * cc + 1))
                    pe.wait_ge(f.mul, it * 6 + (f.hidden + jj + 1))
                    s = (first_slot[parity] + 2 * cc) % RING
                    before_done = jj == 0 or (cc == 1 and jobs[jj - 1] == (0, NTG - 1))
                    project(s, tg, A[jj % 3], None, before_done, (ready, tg * KC) if cc == 0 and ready else None)
                    project(s + 1, tg, B[jj % 3], f.up, tg == NTG - 1)

            def down_tile(s, parity, c, tg, n, it, release):
                pe.wait_ge(f.add, it * 24 + (f.outs + n + 1))
                first = True
                for kk in range(2):
                    w = slice(((c % 4) * 2 + kk) * P, ((c % 4) * 2 + kk + 1) * P)
                    for i, (a, b) in enumerate(((wh, hh), (wh, hl), (wl, hh))):
                        mm = pe.matmul(DN[n % 2][:, 0:TG], a[:, s + c // 4, w], b[:, 2 * parity + kk, tgs(tg)],
                                       start=first, stop=(kk == 1 and i == 2))
                        if first and release:
                            mm.then_inc(w_done, 1)
                        first = False
                mm.then_inc(f.down, 1)

            def down(it, unit, s, parity):
                pe.wait_ge(f.lo, it * 6 + (f.hidden + 8))
                for c in range(KC):
                    if c % 4 == 0:
                        unit_ready(unit + c // 4)
                    for tg in range(NTG):
                        down_tile(s, parity, c, tg, c * NTG + tg, it, c % 4 == 0 and tg == 0)

            s0 = first_unit % RING
            first_slot = {0: s0}
            gate_up(0, first_unit, 0, n_in.ready)
            with pe.Fori(0, NG // 2) as it:
                base = it * 12 + (first_unit + 4)
                first_slot = {1: s0, 0: (s0 + 2) % RING}
                gate_up(it * 2 + 1, base, 1, None)
                down(it * 2, base + 4, s0, 0)
                gate_up(it * 2 + 2, base + 6, 0, None)
                down(it * 2 + 1, base + 10, (s0 + 2) % RING, 1)
            unit = first_unit + 3 * FC - 2
            unit_ready(unit)
            unit_ready(unit + 1)
            pe.wait_ge(f.lo, f.hidden + (NG - 1) * 6 + 8)
            for tg in range(NTG):
                for c in range(KC):
                    release = (tg == 0 and c == 0) or (tg == NTG - 1 and c == KC // 2)
                    down_tile(s0, 0, c, tg, tg * KC + c, NG - 1, release)
                if tg:
                    mean_square(n_next, tg - 1, B[tg - 1], tg * KC)
            mean_square(n_next, NTG - 1, B[NTG - 1], NTG * KC)

        ffn(f0, U_FFN0, n_ffn0, n_kv)

        linear(l_k, U_K, PAIR_FIRST, n_kv.ready)

        def turn(c):
            pe.wait_ge(l_v.out, l_v.base + 6 + tiles_until(PAIR_LAST, c))
            for i in range(3):
                n = 3 * c + i
                pe.wait_ge(v_copy, n + 1)
                for b in range(4 * i, min(4 * i + 4, 9)):
                    rows = min(P, T - b * P)
                    mm = pe.transpose(DN[n % 2][0:rows, (b % 4) * P:(b % 4 + 1) * P],
                                      stage[:, c % 2, b * P:b * P + rows], ident[:])
                mm.then_inc(v_turn, 1)

        linear(l_v, U_V, PAIR_LAST, None, lambda j: turn(j // NTG - 1) if j % NTG == 0 and 0 < j <= 3 * (KC - 2) else None)
        linear(l_q, U_Q, PAIR_FIRST, n_mix1.ready, lambda j: (turn(KC - 2), turn(KC - 1)) if j == 5 else None)

        def att_z(it, t):
            s, g = STEPS[t], it * NSTEP + t
            e, c0 = s["e"], s["c0"]
            if t % HSTEP == 0:
                pe.wait_ge(Att.k_in[e], it * 16 + 16)
            if s["first"]:
                pe.wait_ge(Att.q_in[s["qt"]], it * 96 + 48 * (e + 1))
            pe.wait_ge(Att.a, g + 1)
            keys = slice(s["b"] * P, (s["b"] + 1) * P)
            cols = slice(s["qt"] * QT + c0, (s["qt"] + 1) * QT)
            pe.matmul(Z[t % NZ][:, c0:QT], k_sb[:, e, keys], qh_sb[:, cols], start=True, stop=False)
            pe.matmul(Z[t % NZ][:, c0:QT], k_sb[0:DH, e, keys], ql_sb[:, cols], start=False, stop=True)\
              .then_inc(Att.z, 1)

        def att_cum(it, t):
            s, g = STEPS[t], it * NSTEP + t
            c0, cr = s["c0"], s["carry0"]
            pe.wait_ge(Att.sl, g + 4)
            for part in (sh_sb, sl_sb):
                mm = pe.matmul(Z[t % NZ][:, c0:QT], neg_tri_r[:], part[:, t % 3, c0:QT], start=False, stop=True,
                               skip_group_check=True)
            if not s["first"]:
                pe.wait_ge(Att.block, it * NBLOCK + STEPS[t - 1]["blocks"])
                if not STEPS[t - 1]["first"]:
                    pe.wait_ge(Att.carry, it * NCARRY + (STEPS[t - 1]["carries"] + 2))
                mm = pe.matmul(Z[t % NZ][:, cr:QT], neg_one[:], carry[t % 4][:, cr:QT], start=False, stop=True,
                               skip_group_check=True)
            mm.then_inc(Att.cum, 1)

        def att_av(it, t):
            s, g = STEPS[t], it * NSTEP + t
            e, c0 = s["e"], s["c0"]
            if t % HSTEP == 0:
                pe.wait_ge(Att.v_in[e], it * 32 + 32)
            if s["first"]:
                pe.wait_ge(Att.o_lo, it * 4 + (2 * e + s["qt"] + 1))
            if s["diag"]:
                pe.wait_ge(Att.a_mask, it * NMASK + s["masks"])
            else:
                pe.wait_ge(Att.a, g + 1 + NZ)
            rows = slice(DH * e, DH * e + DH)
            pe.matmul(DN[s["qt"]][rows, c0:QT], v_sb[:, e, s["b"], :], a_sb[:, t % 3, c0:QT],
                      start=s["first"], stop=s["last"], skip_group_check=True).then_inc(Att.av, 1)

        pe.wait_ge(consts, 8)
        pe.wait_ge(l_q.out, l_q.base + 6 + NTG * KC)
        attention_slots(pe, ((att_z, 6), (att_cum, 2), (att_av, 0)))

        pe.wait_ge(Dec.new_in, 48)
        pe.wait_ge(Dec.one, 1)
        for i, rows in ((0, P), (1, P), (2, NS)):
            pe.matmul(Z[i][0:rows, :], one_row[0:1, 0:rows], b_dec[:], start=True, stop=True)
        for n in range(2 * NB):
            b, j = divmod(n, 2)
            pe.wait_ge(Dec.k_in[n % 4], 16 * (n // 4 + 1))
            for c in range(KC):
                cols = slice(c * NB * 8 + b * 8, c * NB * 8 + b * 8 + 8)
                mm = pe.matmul(Z[j][:, cols], kp[:, n % 4, c], q_dec[:, c, b], start=False, stop=True,
                               skip_group_check=True)
            mm.then_inc(Dec.kz, 1)
        for c in range(KC):
            mm = pe.matmul(Z[2][0:NS, c * 64:(c + 1) * 64], kn[:, c, :], q_dec[:, c].rearrange("p b q -> p (b q)"),
                           start=False, stop=True, skip_group_check=True)
        mm.then_inc(Dec.z, 1)
        pe.wait_ge(Dec.s_mask, 2 * KC)
        pe.matmul(Z[2][0:NS, :], neg_tri[0:NS, 0:NS], ds_sb[0:NS, 2], start=False, stop=True,
                  skip_group_check=True).then_inc(Dec.cum, 1)
        pe.wait_ge(Dec.s, 3)
        pe.matmul(Z[1][:, :], neg_tri[:], ds_sb[:, 1], start=False, stop=True, skip_group_check=True)
        pe.matmul(Z[1][:, :], neg_one[0:NS, :], ds_sb[0:NS, 2], start=False, stop=True,
                  skip_group_check=True).then_inc(Dec.cum, 1)
        pe.matmul(Z[0][:, :], neg_tri[:], ds_sb[:, 0], start=False, stop=True, skip_group_check=True)
        pe.matmul(Z[0][:, :], neg_one[:], ds_sb[:, 1], start=False, stop=True, skip_group_check=True)
        pe.matmul(Z[0][:, :], neg_one[0:NS, :], ds_sb[0:NS, 2], start=False, stop=True,
                  skip_group_check=True).then_inc(Dec.cum, 1)
        pe.wait_ge(Dec.a, 3)
        pe.wait_ge(Dec.a_mask, 2 * KC)
        for c in range(KC):
            pe.matmul(DN[0][:, c * 64:(c + 1) * 64], vnew[:, c * P:(c + 1) * P], da_sb[0:NS, 2, c * 64:(c + 1) * 64],
                      start=(c == 0), stop=True, skip_group_check=True)
        for n in range(2 * NB):
            b, j = divmod(n, 2)
            pe.wait_ge(Dec.v_in[n % 4], 16 * (n // 4 + 1))
            for c in range(KC):
                cols = slice(c * NB * 8 + b * 8, c * NB * 8 + b * 8 + 8)
                mm = pe.matmul(DN[0][:, cols], vp[:, n % 4, c * P:(c + 1) * P], da_sb[:, j, cols], start=False,
                               stop=True, skip_group_check=True)
            mm.then_inc(Dec.pv, 1)

        pe.wait_ge(Dec.o_lo, 2)
        residual_linear(l_o, U_O, None, n_ffn1)
        ffn(f1, U_FFN1, n_ffn1, n_fin)

    ctx.close()


def _units(w):
    return w.reshape(KC, P, -1, P).transpose(2, 1, 0, 3).reshape(-1, P, KC * P)


def _ffn_units(gate, up, down):
    gu = np.stack([_units(gate), _units(up)], axis=1).reshape(NG, 4, P, KC * P)
    dn = down.reshape(NG, 2, P, 2, 4, P).transpose(0, 3, 2, 4, 1, 5).reshape(NG, 2, P, KC * P)
    parts = [gu[0]]
    for g in range(1, NG):
        parts += [gu[g], dn[g - 1]]
    return np.concatenate(parts + [dn[NG - 1]])


def _cols(v):
    return v.reshape(-1, P).T


def kernel(x_prompt, x_sample, state_conv, cache_k, cache_v, page_table, norm_mix, norm_ffn, conv_w_pw1, conv_b_pw1,
           conv_w_dw, conv_b_dw, conv_ln_g, conv_ln_b, conv_w_pw2, conv_b_pw2, kv_norm, w_kv, w_q, w_o, b_logit,
           ffn_w_gate, ffn_w_up, ffn_w_down, final_norm):
    import concourse.bacc as bacc
    from concourse.bass_utils import run_bass_kernel_spmd

    a = [np.asarray(v) for v in (x_prompt, x_sample, state_conv, cache_k, cache_v, page_table, norm_mix, norm_ffn,
                                 conv_w_pw1, conv_b_pw1, conv_w_dw, conv_b_dw, conv_ln_g, conv_ln_b, conv_w_pw2,
                                 conv_b_pw2, kv_norm, w_kv, w_q, w_o, b_logit, ffn_w_gate, ffn_w_up, ffn_w_down,
                                 final_norm)]
    (x_prompt, x_sample, state_conv, cache_k, cache_v, page_table, norm_mix, norm_ffn, conv_w_pw1, conv_b_pw1,
     conv_w_dw, conv_b_dw, conv_ln_g, conv_ln_b, conv_w_pw2, conv_b_pw2, kv_norm, w_kv, w_q, w_o, b_logit,
     ffn_w_gate, ffn_w_up, ffn_w_down, final_norm) = a

    pw1 = _units(conv_w_pw1[0])
    pw1 = np.stack([pw1[:KC], pw1[KC:]], axis=1).reshape(2 * KC, P, KC * P)
    wstream = np.concatenate([
        pw1, _units(conv_w_pw2[0]), _ffn_units(ffn_w_gate[0], ffn_w_up[0], ffn_w_down[0]), _units(w_kv),
        _units(w_q[0]), _units(w_o[0]), _ffn_units(ffn_w_gate[1], ffn_w_up[1], ffn_w_down[1])])
    params = np.concatenate([
        _cols(norm_mix[0]), _cols(norm_ffn[0]), _cols(kv_norm), _cols(norm_mix[1]), _cols(norm_ffn[1]),
        _cols(final_norm), _cols(conv_b_pw1[0]), _cols(conv_b_dw[0]), _cols(conv_ln_g[0]), _cols(conv_ln_b[0]),
        _cols(conv_b_pw2[0]), conv_w_dw[0].reshape(W, KC, P).transpose(2, 1, 0).reshape(P, KC * W)], axis=1)
    state = np.zeros((P, KC, NB, SLOT), np.float32)
    state[..., :PAD] = state_conv[0].reshape(NB, PAD, KC, P).transpose(3, 2, 0, 1)
    n_phys = cache_k.shape[0]
    ins = {
        "x_t": np.concatenate([x_prompt.reshape(SEQ, D), x_sample.reshape(NS, D)]).T,
        "params": params,
        "wstream": wstream,
        "conv_state": state,
        "cache_kt": cache_k.reshape(n_phys, P, KC, P).transpose(0, 3, 2, 1),
        "cache_v": cache_v.reshape(n_phys, P, D),
        "page_table": page_table.reshape(1, 2 * NB),
        "bias_row": np.broadcast_to(b_logit[0][:, None], (H, P)),
        "bias_dec": np.broadcast_to(b_logit[0].reshape(KC, 1, 2, 1), (KC, NB, 2, NQ)).reshape(1, QT),
    }
    outs = {"y_t": (D, T), "u_tail": (KC, P, PAD), "us_tail": (P, KC, NB, SLOT), "k_t": (D, T), "v_nat": (T, D)}

    nc = bacc.Bacc("TRN2", target_bir_lowering=False, num_devices=1)
    ins = {name: np.ascontiguousarray(v) for name, v in ins.items()}
    args = [nc.dram_tensor(name, v.shape, mybir.dt.from_np(v.dtype), kind="ExternalInput").ap()
            for name, v in ins.items()]
    args += [nc.dram_tensor(name, shape, F32, kind="ExternalOutput").ap() for name, shape in outs.items()]
    args += [nc.dram_tensor(name, (H, 2, DH, SEQ), F32, kind="Internal").ap() for name in ("k_split", "q_split")]
    build(nc, *args)
    r = run_bass_kernel_spmd(nc, [ins], core_ids=[0]).results[0]

    y = r["y_t"].T
    u_tail = r["u_tail"].reshape(D, PAD).T
    us = r["us_tail"][..., NQ:].transpose(2, 3, 1, 0).reshape(NB, PAD, D)
    k = r["k_t"].T
    v = r["v_nat"]
    return (y[:SEQ].reshape(1, SEQ, D), y[SEQ:].reshape(NB, NQ, D), u_tail.reshape(1, 1, PAD, D),
            us.reshape(1, NB, PAD, D), k[:SEQ].reshape(1, SEQ, H, DH), v[:SEQ].reshape(1, SEQ, H, DH),
            k[SEQ:].reshape(NB, NQ, H, DH), v[SEQ:].reshape(NB, NQ, H, DH))
```
